# Optimizing a Trainium2 kernel written in Bass

```python
import functools
import jax, jax.numpy as jnp
from jax import lax
import numpy as np

D_MODEL = 2048
BATCH = 1
SEQ = 256
DEPTH = 1
DEC_BATCH = 8
DEC_SEQ = 4
PAST_LEN = 2048
PAGE_SIZE = 128

N_META = 16
ATTN_WIDTH = D_MODEL // 2
N_HEADS = 8
HEAD_DIM = ATTN_WIDTH // N_HEADS
N_KV_HEADS = 4
ROT_DIM = HEAD_DIM // 4
N_IDX_HEADS = 8
IDX_DIM = 64
IDX_ROT_DIM = IDX_DIM // 4
TOPK_MAX = 256
POOL_WIDTH = D_MODEL - ATTN_WIDTH
POOL_WINDOWS = (2, 4, 8, 16)
POOL_GROUP = POOL_WIDTH // len(POOL_WINDOWS)
POOL_CTX = max(POOL_WINDOWS) - 1
MIX_WIDTH = ATTN_WIDTH + POOL_WIDTH
D_FF = 5632
CONV_WIDTH = 3
ROPE_THETA = 500000.0
Q_BLOCK = 128
LN_EPS = 1e-5
DEEPNORM_ALPHA = (2.0 * DEPTH) ** 0.25
DEEPNORM_BETA = (8.0 * DEPTH) ** -0.25
IN_SIZES = (N_HEADS * HEAD_DIM, N_KV_HEADS * HEAD_DIM, N_KV_HEADS * HEAD_DIM,
            N_IDX_HEADS * IDX_DIM, IDX_DIM, N_IDX_HEADS, POOL_WIDTH)
IN_WIDTH = sum(IN_SIZES)
IN_OFFSETS = tuple(int(o) for o in np.cumsum(IN_SIZES)[:-1])

kernel_name = "hymba_dsa_pool_convffn_deepnorm_step"

def layer_norm(x, g, b):
    xf = x.astype(jnp.float32)
    mu = jnp.mean(xf, axis=-1, keepdims=True)
    var = jnp.mean(jnp.square(xf - mu), axis=-1, keepdims=True)
    y = (xf - mu) * lax.rsqrt(var + LN_EPS) * g.astype(jnp.float32) + b.astype(jnp.float32)
    return y.astype(x.dtype)

def rope_partial(x, pos, rot_dim):
    half = rot_dim // 2
    inv_freq = ROPE_THETA ** (-jnp.arange(half, dtype=jnp.float32) / half)
    ang = pos.astype(jnp.float32)[:, None] * inv_freq[None, :]
    cos = jnp.cos(ang)[:, None, :]
    sin = jnp.sin(ang)[:, None, :]
    xr = x[..., :rot_dim].astype(jnp.float32)
    x1, x2 = xr[..., :half], xr[..., half:]
    rot = jnp.concatenate([x1 * cos - x2 * sin, x2 * cos + x1 * sin], axis=-1).astype(x.dtype)
    return jnp.concatenate([rot, x[..., rot_dim:]], axis=-1)

def split_proj(x, w_in):
    h = jnp.einsum('btd,de->bte', x, w_in)
    B, T, _ = h.shape
    q, k, v, iq, ik, iw, p = jnp.split(h, IN_OFFSETS, axis=-1)
    return (q.reshape(B, T, N_HEADS, HEAD_DIM), k.reshape(B, T, N_KV_HEADS, HEAD_DIM),
            v.reshape(B, T, N_KV_HEADS, HEAD_DIM), iq.reshape(B, T, N_IDX_HEADS, IDX_DIM),
            ik, iw, p)

def index_scores(iq, iw, ik):
    s = jnp.einsum('bqhd,bsd->bqhs', iq, ik).astype(jnp.float32) * (IDX_DIM ** -0.5)
    w = iw.astype(jnp.float32) * (N_IDX_HEADS ** -0.5)
    return jnp.einsum('bqhs,bqh->bqs', jax.nn.relu(s), w)

def gather_rows(rows, idx):
    return jax.vmap(lambda r, i: r[i])(rows, idx)

def sparse_attend(q, k_sel, v_sel, valid):
    B, Q, H, Dh = q.shape
    kvh = k_sel.shape[3]
    qg = q.reshape(B, Q, kvh, H // kvh, Dh)
    s = jnp.einsum('bqgrd,bqkgd->bqgrk', qg, k_sel).astype(jnp.float32) * (Dh ** -0.5)
    s = jnp.where(valid[:, :, None, None, :], s, -jnp.inf)
    p = jax.nn.softmax(s, axis=-1).astype(v_sel.dtype)
    o = jnp.einsum('bqgrk,bqkgd->bqgrd', p, v_sel)
    return o.reshape(B, Q, H * Dh)

def prompt_attention(q, k, v, iq, ik, iw, topk):
    B, T = q.shape[:2]
    nb = -(-T // Q_BLOCK)
    pad = nb * Q_BLOCK - T
    key_pos = jnp.arange(T)

    def to_blocks(a):
        a = jnp.pad(a, [(0, 0), (0, pad)] + [(0, 0)] * (a.ndim - 2))
        return a.reshape((B, nb, Q_BLOCK) + a.shape[2:]).swapaxes(0, 1)

    def one_block(args):
        qb, iqb, iwb, pb = args
        score = index_scores(iqb, iwb, ik)
        score = jnp.where(key_pos[None, None, :] <= pb[None, :, None], score, -jnp.inf)
        _, idx = lax.top_k(score, topk)
        valid = idx <= pb[None, :, None]
        return sparse_attend(qb, gather_rows(k, idx), gather_rows(v, idx), valid)

    blocks_pos = jnp.arange(nb * Q_BLOCK).reshape(nb, Q_BLOCK)
    out = lax.map(one_block, (to_blocks(q), to_blocks(iq), to_blocks(iw), blocks_pos))
    return out.swapaxes(0, 1).reshape(B, nb * Q_BLOCK, -1)[:, :T]

def sample_attention(q, k, v, iq, ik, iw, pos, cache_k, cache_v, cache_idx_k, page_table, topk):
    DB, Q = q.shape[:2]
    past_ik = cache_idx_k[page_table].reshape(DB, PAST_LEN, IDX_DIM)
    ik_all = jnp.concatenate([past_ik, ik.astype(past_ik.dtype)], axis=1)
    key_pos = jnp.arange(PAST_LEN + Q)
    score = index_scores(iq, iw, ik_all)
    score = jnp.where(key_pos[None, None, :] <= pos[None, :, None], score, -jnp.inf)
    _, idx = lax.top_k(score, topk)
    valid = idx <= pos[None, :, None]
    in_past = idx < PAST_LEN
    ip = jnp.minimum(idx, PAST_LEN - 1)
    phys = jax.vmap(lambda pt, pg: pt[pg])(page_table, ip // PAGE_SIZE)
    off = ip % PAGE_SIZE
    inew = jnp.clip(idx - PAST_LEN, 0, Q - 1)
    sel = in_past[..., None, None]
    k_sel = jnp.where(sel, cache_k[phys, off], gather_rows(k, inew).astype(cache_k.dtype))
    v_sel = jnp.where(sel, cache_v[phys, off], gather_rows(v, inew).astype(cache_v.dtype))
    return sparse_attend(q.astype(k_sel.dtype), k_sel, v_sel, valid)

def multiscale_pool(p_ext, pos):
    Q = pos.shape[0]
    n_ctx = p_ext.shape[1] - Q
    B, _, C = p_ext.shape
    cs = jnp.concatenate([jnp.zeros((B, 1, C), jnp.float32),
                          jnp.cumsum(p_ext.astype(jnp.float32), axis=1)], axis=1)
    hi = cs[:, n_ctx + 1:]
    x_self = p_ext[:, n_ctx:].astype(jnp.float32)
    outs = []
    for g, w in enumerate(POOL_WINDOWS):
        c0, c1 = g * POOL_GROUP, (g + 1) * POOL_GROUP
        lo = cs[:, n_ctx + 1 - w: n_ctx + 1 - w + Q, c0:c1]
        cnt = jnp.minimum(w, pos + 1).astype(jnp.float32)[None, :, None]
        outs.append((hi[:, :, c0:c1] - lo) / cnt - x_self[:, :, c0:c1])
    return jnp.concatenate(outs, axis=-1).astype(p_ext.dtype)

def conv_ffn(x, u_prefix, w_up, conv_w, conv_b, w_down):
    u = jnp.einsum('btd,de->bte', x, w_up)
    u_ext = jnp.concatenate([u_prefix.astype(u.dtype), u], axis=1)
    Q = u.shape[1]
    c = conv_b
    for j in range(CONV_WIDTH):
        c = c + conv_w[j] * u_ext[:, j:j + Q]
    gate, val = jnp.split(c, 2, axis=-1)
    h = jax.nn.silu(gate) * val
    return jnp.einsum('btf,fd->btd', h, w_down), u_ext[:, -(CONV_WIDTH - 1):]

def trunk_layer(x, pos, pool_prefix, conv_prefix, attend, w_in, w_pool, pool_scale, w_out,
                ln1_g, ln1_b, w_up, conv_w, conv_b, w_down, ln2_g, ln2_b):
    q, k, v, iq, ik, iw, p = split_proj(x, w_in)
    q = rope_partial(q, pos, ROT_DIM)
    k = rope_partial(k, pos, ROT_DIM)
    iq = rope_partial(iq, pos, IDX_ROT_DIM)
    ik = rope_partial(ik[:, :, None, :], pos, IDX_ROT_DIM)[:, :, 0]
    a = attend(q, k, v, iq, ik, iw).astype(x.dtype)
    p_ext = jnp.concatenate([pool_prefix.astype(p.dtype), p], axis=1)
    pooled = multiscale_pool(p_ext, pos)
    B, Q, _ = pooled.shape
    m = jnp.einsum('bqgc,gce->bqge', pooled.reshape(B, Q, len(POOL_WINDOWS), POOL_GROUP),
                   w_pool).reshape(B, Q, POOL_WIDTH) * pool_scale
    mix = jnp.einsum('bqm,md->bqd', jnp.concatenate([a, m], axis=-1), w_out)
    x = layer_norm(DEEPNORM_ALPHA * x + mix, ln1_g, ln1_b)
    f, conv_state = conv_ffn(x, conv_prefix, w_up, conv_w, conv_b, w_down)
    x = layer_norm(DEEPNORM_ALPHA * x + f, ln2_g, ln2_b)
    return x, k, v, ik, p_ext[:, -POOL_CTX:], conv_state

def setup_inputs(seed: int = 0) -> dict:
    key = jax.random.key(seed)
    ks = jax.random.split(key, 24)
    n_pages = PAST_LEN // PAGE_SIZE
    n_used = DEC_BATCH * n_pages
    n_phys = n_used + max(1, n_used // 4)
    nrm = jax.random.normal
    f32 = jnp.float32
    page_table = jax.random.permutation(ks[0], n_phys)[:n_used].reshape(DEC_BATCH, n_pages).astype(jnp.int32)
    return {
        "x_prompt": nrm(ks[1], (BATCH, SEQ, D_MODEL), f32),
        "x_sample": nrm(ks[2], (DEC_BATCH, DEC_SEQ, D_MODEL), f32),
        "cache_k": nrm(ks[3], (DEPTH, n_phys, PAGE_SIZE, N_KV_HEADS, HEAD_DIM), f32),
        "cache_v": nrm(ks[4], (DEPTH, n_phys, PAGE_SIZE, N_KV_HEADS, HEAD_DIM), f32),
        "cache_idx_k": nrm(ks[5], (DEPTH, n_phys, PAGE_SIZE, IDX_DIM), f32),
        "state_pool": nrm(ks[6], (DEPTH, DEC_BATCH, POOL_CTX, POOL_WIDTH), f32),
        "state_conv": nrm(ks[7], (DEPTH, DEC_BATCH, CONV_WIDTH - 1, 2 * D_FF), f32),
        "page_table": page_table,
        "meta_tokens": nrm(ks[8], (N_META, D_MODEL), f32),
        "w_in": nrm(ks[9], (DEPTH, D_MODEL, IN_WIDTH), f32) * D_MODEL ** -0.5,
        "w_pool": nrm(ks[10], (DEPTH, len(POOL_WINDOWS), POOL_GROUP, POOL_GROUP), f32) * POOL_GROUP ** -0.5,
        "pool_scale": 1.0 + 0.02 * nrm(ks[11], (DEPTH, POOL_WIDTH), f32),
        "w_out": nrm(ks[12], (DEPTH, MIX_WIDTH, D_MODEL), f32) * (MIX_WIDTH ** -0.5) * DEEPNORM_BETA,
        "ln1_g": 1.0 + 0.02 * nrm(ks[13], (DEPTH, D_MODEL), f32),
        "ln1_b": 0.01 * nrm(ks[14], (DEPTH, D_MODEL), f32),
        "w_up": nrm(ks[15], (DEPTH, D_MODEL, 2 * D_FF), f32) * D_MODEL ** -0.5,
        "conv_w": nrm(ks[16], (DEPTH, CONV_WIDTH, 2 * D_FF), f32) * CONV_WIDTH ** -0.5,
        "conv_b": 0.01 * nrm(ks[17], (DEPTH, 2 * D_FF), f32),
        "w_down": nrm(ks[18], (DEPTH, D_FF, D_MODEL), f32) * (D_FF ** -0.5) * DEEPNORM_BETA,
        "ln2_g": 1.0 + 0.02 * nrm(ks[19], (DEPTH, D_MODEL), f32),
        "ln2_b": 0.01 * nrm(ks[20], (DEPTH, D_MODEL), f32),
    }

def reference(x_prompt, x_sample, cache_k, cache_v, cache_idx_k, state_pool, state_conv, page_table,
              meta_tokens, w_in, w_pool, pool_scale, w_out, ln1_g, ln1_b, w_up, conv_w, conv_b,
              w_down, ln2_g, ln2_b):
    B, S, D = x_prompt.shape
    DB, QS, _ = x_sample.shape
    T = N_META + S
    xp = jnp.concatenate([jnp.broadcast_to(meta_tokens.astype(x_prompt.dtype)[None], (B, N_META, D)),
                          x_prompt], axis=1)
    xs = x_sample
    pos_p = jnp.arange(T)
    pos_s = PAST_LEN + jnp.arange(QS)
    topk_p = min(TOPK_MAX, S // 4)
    topk_s = min(TOPK_MAX, (PAST_LEN + QS) // 4)
    kp_l, vp_l, ikp_l, poolp_l, convp_l = [], [], [], [], []
    ks_l, vs_l, iks_l, pools_l, convs_l = [], [], [], [], []
    for l in range(DEPTH):
        lw = (w_in[l], w_pool[l], pool_scale[l], w_out[l], ln1_g[l], ln1_b[l],
              w_up[l], conv_w[l], conv_b[l], w_down[l], ln2_g[l], ln2_b[l])
        attend_p = functools.partial(prompt_attention, topk=topk_p)
        attend_s = functools.partial(sample_attention, pos=pos_s, cache_k=cache_k[l], cache_v=cache_v[l],
                                     cache_idx_k=cache_idx_k[l], page_table=page_table, topk=topk_s)
        xp, kp, vp, ikp, poolp, convp = trunk_layer(
            xp, pos_p, jnp.zeros((B, POOL_CTX, POOL_WIDTH), xp.dtype),
            jnp.zeros((B, CONV_WIDTH - 1, 2 * D_FF), xp.dtype), attend_p, *lw)
        xs, ks_, vs_, iks, pools, convs = trunk_layer(
            xs, pos_s, state_pool[l], state_conv[l], attend_s, *lw)
        kp_l.append(kp); vp_l.append(vp); ikp_l.append(ikp); poolp_l.append(poolp); convp_l.append(convp)
        ks_l.append(ks_); vs_l.append(vs_); iks_l.append(iks); pools_l.append(pools); convs_l.append(convs)
    y_prompt = xp[:, N_META:]
    return (y_prompt, xs,
            jnp.stack(kp_l), jnp.stack(vp_l), jnp.stack(ikp_l), jnp.stack(poolp_l), jnp.stack(convp_l),
            jnp.stack(ks_l), jnp.stack(vs_l), jnp.stack(iks_l), jnp.stack(pools_l), jnp.stack(convs_l))


_drawn_inputs = setup_inputs


def setup_inputs(seed=0):
    import zlib

    import numpy as np

    out = dict(_drawn_inputs(seed))
    spreads = {}
    factors = {'pool_scale': 23.284,
     'ln1_b': 5.338,
     'conv_b': 8.0,
     'ln2_g': 8.421,
     'ln2_b': 16.681,
     'cache_k': 5.223,
     'cache_v': 4.117,
     'cache_idx_k': 4.386}
    for name, (base, spread) in spreads.items():
        noise = np.random.default_rng([zlib.crc32(name.encode()), seed]).standard_normal(out[name].shape)
        drawn = base * np.exp(spread * noise) if base else spread * noise
        out[name] = __import__('jax').numpy.asarray(drawn.astype(out[name].dtype))
    for name, factor in factors.items():
        out[name] = (out[name] * factor).astype(out[name].dtype)
    return out
```

```python
import numpy as np
import concourse.bass as bass
from concourse import mybir
from contextlib import ExitStack

D = 2048
META, SEQ, DB, DQ = 16, 256, 8, 4
TP = META + SEQ
TS = DB * DQ
T = TP + TS
NH, KVH, HD = 8, 4, 128
IH, ID = 8, 64
PAST, PAGE = 2048, 128
NPG = PAST // PAGE
NPAGES = DB * NPG
NPHYS = NPAGES + NPAGES // 4
TOPK_P = min(256, SEQ // 4)
TOPK_S = min(256, (PAST + DQ) // 4)
PW, WINS = 1024, (2, 4, 8, 16)
CTX = 15
DFF = 5632
THETA = 500000.0
EPS = 1e-5
ALPHA = 2.0 ** 0.25
SCALE = HD ** -0.5
NEG = float(np.finfo(np.float32).min)
FAR = 1.0e30

KB = D // 128
FB = DFF // 128
CK, CW = 2, 512
RING = 3

NX = KB // CK
IQ0 = NX
IK0 = IQ0 + 8
IKW = ID + IH
IN0, NIN = IK0 + 2, 6
OUT0, NOUT = IN0 + 8 * NIN, 4
UP0, NUP = OUT0 + 8 * NOUT, DFF // 256
DN0, NDN = UP0 + 8 * NUP, 4
DNC = FB // CK
END = DN0 + DNC * NDN
POOL_LO = (IN0 + 8, OUT0)
LO_GAP = POOL_LO[1] - POOL_LO[0]
SLAB_OUT, SLAB_UP = 1 + NIN, 1 + NIN + NOUT
SLAB_DN = SLAB_UP + NUP

KR = 8
VX, VR = 17, 25
P_EXT = CTX + TP + DB * (CTX + DQ)
PS0 = CTX + TP
P_OUT = PS0 - CTX
U_EXT = 2 + TP + DB * (2 + DQ) + 4
US0 = 2 + TP
UO = 2 + TP + DB * (2 + DQ) - 2
TOK = ((0, 128), (128, 128), (256, 16), (272, 32))
PQ = ((0, 128, 128, 0), (128, 128, 256, 128), (256, 16, 272, 384))


def position(n):
    if n < IK0:
        return n % 8
    if n < IN0:
        return n - IK0
    if n < DN0:
        return (n - IN0) % 8
    return (n - DN0) % (2 * DNC)


def back(c):
    return 2 if c < 2 else 3


def loads(n):
    return sum(1 for m in range(n + 1) if position(m) % RING == position(n) % RING)


def per_slab(c):
    return sum(1 for k in range(8) if k % RING == c % RING)


def layer(nc, xT, w_iq, w_ik, w_in, w_out, w_up, w_down, kT_cache, v_cache, ik_cache, pages,
          pool_ctx, conv_ctx, w_pool, pool_scale, ln1, ln2, conv_p,
          ident_c, e8_c, sel_c, new_c, rope_c, count_c,
          yT, kT_out, vT_out, ikT_out, pT_out, cT_out):
    f32, f32r, i32 = mybir.dt.float32, mybir.dt.float32r, mybir.dt.int32
    ALU, ACT, AX = mybir.AluOpType, mybir.ActivationFunctionType, mybir.AxisListType

    at = [-(-nc.sbuf_base // 32) * 32]

    def region(size):
        start = at[0]
        at[0] += -(-size // 32) * 32
        return start

    def put(name, shape, dt=f32, where=None):
        if where is None:
            where = region(4 * int(np.prod(shape[1:])))
        return nc.alloc_sbuf_tensor_at(name, shape, dt, offset=where)

    xr = region(2 * KB * T * 4)
    x_hi = put("x_hi", [128, KB, T], f32r, xr)
    x_lo = put("x_lo", [128, KB, T], f32r, xr + KB * T * 4)
    v_ring_x = put("v_ring_x", [128, VX, 512], f32, xr)
    mask_s = put("mask_s", [128, NPG + 1, TS], f32, xr + VX * 2048)
    smax = put("smax", [128, DB * 32], f32, xr + VX * 2048 + 2176)
    raw_at = region(RING * CK * CW * 4)
    raw = put("raw", [128, RING, CK * CW], f32, raw_at)
    ln_b = put("ln_b", [128, 4, 304], f32, raw_at)
    w_hi = put("w_hi", [128, RING, CK * CW], f32r)
    w_lo = put("w_lo", [128, RING, CK * CW], f32r)
    ident = put("ident", [128, 128])
    ones = put("ones", [128, 128])
    ln1_sb = put("ln1_sb", [128, 2, KB])
    ln2_sb = put("ln2_sb", [128, 2, KB])
    psc = put("psc", [128, 8])
    tiny = put("tiny", [128, 16])
    top8 = put("top8", [128, 8])
    pt_sb = put("pt_sb", [1, NPAGES], i32)
    sel_sb = put("sel_sb", [128, 2, TS])
    wsel = put("wsel", [128, 2, TS])
    e8_sb = put("e8_sb", [IH, 128])
    new_sb = put("new_sb", [TS, 2, TS])
    wtok = put("wtok", [128, 3, IH])
    cnt = put("cnt", [128, 4, 16])

    second = at[0]
    r1 = region(2 * 8 * T * 4)
    score = put("score", [TS, PAST + TS], f32, r1)
    work = put("work", [TS, PAST + TS], f32, r1 + 4 * (PAST + TS))
    m_hi = put("m_hi", [128, 8, T], f32r, r1)
    m_lo = put("m_lo", [128, 8, T], f32r, r1 + 8 * T * 4)
    r2 = region(KB * T * 4)
    relu_s = put("relu_s", [128, 2, 2, 512], f32, r2)
    rope_i = put("rope_i", [128, 2, T], f32, r2 + 8192)
    iw_t = put("iw_t", [IH, T], f32, r2 + 8192 + 2432)
    k_ring = put("k_ring", [128, KR, 512], f32, r2)
    v_ring_k = put("v_ring_k", [128, KR, 512], f32, r2)
    z1 = put("z1", [128, KB, T], f32, r2)
    r3 = region(2 * 8 * T * 4)
    ik_a = put("ik_a", [128, DB, 4, PAGE], f32, r3)
    pooled = put("pooled", [128, 8, T], f32, r3)
    wp_sb = put("wp_sb", [128, 4, 2, 256], f32, r3 + 8 * T * 4)
    a_hi = put("a_hi", [128, 8, T], f32r, r3)
    a_lo = put("a_lo", [128, 8, T], f32r, r3 + 8 * T * 4)
    r4 = region(8 * P_EXT * 4)
    iq_t = put("iq_t", [128, 4, T], f32, r4)
    iq_s = put("iq_s", [128, TS, IH], f32, r4 + 4864)
    relu_p = put("relu_p", [128, 4, TP], f32, r4 + 4864 + 1024)
    p_ext = put("p_ext", [128, 8, P_EXT], f32, r4)
    r5 = region(DB * 544 * 4)
    ik_b = put("ik_b", [128, DB, 4, PAGE], f32, r5)
    s_buf = put("s_buf", [128, DB, 544], f32, r5)
    ln_a = put("ln_a", [128, 4, T], f32, r5)
    q_t = put("q_t", [128, NH, T])
    k_t = put("k_t", [128, KVH, T])
    r6 = region(2 * 3264)
    p_work = put("p_work", [128, 656], f32, r6)
    v_t = put("v_t", [128, KVH, T], f32, r6)
    prob = put("prob", [128, 3, TP], f32, r6)
    prob_t = put("prob_t", [128, 3, TP], f32, r6 + 3264)
    v_tok = put("v_tok", [128, 4, 512])
    r7 = region(2 * P_EXT * 4)
    win = put("win", [128, 2, P_EXT], f32, r7)
    swap = put("swap", [128, T], f32, r7)
    ik_d = put("ik_d", [128, T])
    rope_q = put("rope_q", [32, 2, T])
    p_score = put("p_score", [128, 656])
    assert at[0] <= nc.sbuf_usable_end, at[0]

    at[0] = second
    h_hi = put("h_hi", [128, FB, T], f32r)
    h_lo = put("h_lo", [128, FB, T], f32r)
    c_state = put("c_state", [128, 2 * FB, 18])
    f2 = at[0]
    cp_sb = put("cp_sb", [128, 2 * FB, 4])
    u_ext = put("u_ext", [128, 4, U_EXT])
    conv = put("conv", [128, 4, UO + 2])
    gated = put("gated", [128, 2, UO + 2])
    assert at[0] <= nc.sbuf_usable_end, at[0]
    z2 = put("z2", [128, KB, T], f32, f2)
    assert f2 + KB * T * 4 <= nc.sbuf_usable_end

    with ExitStack() as ctx:
        G = ctx.enter_context(nc.psum_tensor("G", [128, 4, 512], f32))
        A = ctx.enter_context(nc.psum_tensor("A", [128, 4, 512], f32))

        def sem(name):
            return ctx.enter_context(nc.semaphore(name))

        raw_in = [sem(f"raw_in{r}") for r in range(RING)]
        consts_in, late_in, pages_in, ctx_in = sem("consts_in"), sem("late_in"), sem("pages_in"), sem("ctx_in")
        ik_in = [sem("ik_in_a"), sem("ik_in_b")]
        k_in = [sem(f"k_in{r}") for r in range(KR)]
        v_in = [sem(f"v_in{r}") for r in range(VR)]
        x_again, pool_in, conv_in = sem("x_again"), sem("pool_in"), sem("conv_in")
        rows_out, v_out = sem("rows_out"), sem("v_out")
        hi_done, lo_dve, lo_pool, chunk_used = sem("hi_done"), sem("lo_dve"), sem("lo_pool"), sem("chunk_used")
        tile_done, g_free = sem("tile_done"), sem("g_free")
        preset = sem("preset")
        ik_proj, ik_kept, ik_roped, ik_twice = sem("ik_proj"), sem("ik_kept"), sem("ik_roped"), sem("ik_twice")
        iq_roped, iq_packed = sem("iq_roped"), sem("iq_packed")
        iw_turned, wtok_kept, wsel_kept = sem("iw_turned"), sem("wtok_kept"), sem("wsel_kept")
        s_raw, s_relu, s_sum, s_kept = sem("s_raw"), sem("s_relu"), sem("s_sum"), sem("s_kept")
        p_raw, p_relu, p_acc, p_causal = sem("p_raw"), sem("p_relu"), sem("p_acc"), sem("p_causal")
        q_roped, k_roped, v_turned, v_kept = sem("q_roped"), sem("k_roped"), sem("v_turned"), sem("v_kept")
        qk_kept, k_used = sem("qk_kept"), sem("k_used")
        new_done, new_kept = sem("new_done"), sem("new_kept")
        windowed, pool_mm, m_high, m_split = sem("windowed"), sem("pool_mm"), sem("m_high"), sem("m_split")
        p_masked, s_masked = sem("p_masked"), sem("s_masked")
        pa_s, pa_m, pa_e, pa_n = sem("pa_s"), sem("pa_m"), sem("pa_e"), sem("pa_n")
        pa_t, pa_tk, pa_o, pa_hi, pa_lo = sem("pa_t"), sem("pa_tk"), sem("pa_o"), sem("pa_hi"), sem("pa_lo")
        mask_t, mask_kept = sem("mask_t"), sem("mask_kept")
        max_col, max_t, max_diag, max_all = sem("max_col"), sem("max_t"), sem("max_diag"), sem("max_all")
        s_shift, s_exp, s_colsum, s_den = sem("s_shift"), sem("s_exp"), sem("s_colsum"), sem("s_den")
        v_used, sa_o, sa_n, sa_hi, sa_lo = sem("v_used"), sem("sa_o"), sem("sa_n"), sem("sa_hi"), sem("sa_lo")
        mean_mm, centred, squared, var_mm = sem("mean_mm"), sem("centred"), sem("squared"), sem("var_mm")
        sd_done, rstd_done, scaled, normed, x1_hi, x1_lo = (
            sem("sd_done"), sem("rstd_done"), sem("scaled"), sem("normed"), sem("x1_hi"), sem("x1_lo"))
        ctx_put, tail_put, conv_a, conv_v, silu_done, gated_done = (
            sem("ctx_put"), sem("tail_put"), sem("conv_a"), sem("conv_v"), sem("silu_done"), sem("gated_done"))
        h_high, h_split, residual = sem("h_high"), sem("h_split"), sem("residual")
        dve_own, act_own, pool_own = sem("dve_own"), sem("act_own"), sem("pool_own")

        block = ctx.enter_context(nc.Block())

        def wait_lo(eng, n):
            if POOL_LO[0] <= n < POOL_LO[1]:
                eng.wait_ge(lo_pool, n + 1 - POOL_LO[0])
            else:
                eng.wait_ge(lo_dve, n + 1 - (LO_GAP if n >= POOL_LO[1] else 0))

        def wait_used(eng, n):
            if n >= IQ0:
                eng.wait_ge(chunk_used, n + 1 - IQ0)

        def wait_tile(eng, s, j):
            if j < 3:
                eng.wait_ge(tile_done, 3 * s + j + 1)
            else:
                wait_used(eng, (IK0 if s == 0 else IN0 + 8 * s) - 1)

        def samples(ap, width, lo, n):
            return ap.rearrange("p (b w) -> p b w", w=width)[:, :, lo:lo + n]

        @block.sync
        def _(sp):
            def load_chunk(n, src, width=CK * CW):
                c = position(n)
                if n - back(c) >= 0:
                    wait_lo(sp, n - back(c))
                sp.dma_start(raw[:, c % RING, 0:width], src).then_inc(raw_in[c % RING], 16)

            for n in range(NX):
                load_chunk(n, xT[:, CK * T * n:CK * T * (n + 1)], CK * T)
                if n == 2:
                    sp.dma_start(pt_sb[:], pages).then_inc(pages_in, 16)
            for dst, src in ((ident[:], ident_c), (e8_sb[:], e8_c), (sel_sb[:], sel_c), (new_sb[:], new_c),
                             (rope_i[:], rope_c[:, 0:2]), (rope_q[:], rope_c[0:32, 2:4])):
                sp.dma_start(dst, src).then_inc(consts_in, 16)
            sp.wait_ge(pages_in, 16)

            def page_number(j):
                return sp.value_load(pt_sb[0:1, j:j + 1], min_val=0, max_val=NPHYS - 1)

            def load_ik(g, b, i, j):
                r = page_number(NPG * b + 8 * j + 4 * g + i)
                sp.dma_start((ik_a, ik_b)[g][64 * j:64 * j + 64, b, i, :],
                             ik_cache[bass.ds(r, 1)].rearrange("a p n -> p (a n)")).then_inc(ik_in[g], 16)

            order = [(g, b, i, j) for g in range(2) for b in range(DB) for i in range(4) for j in range(2)]
            for n in range(IQ0, IN0 + 8):
                if n < IK0:
                    load_chunk(n, w_iq[:, n - IQ0])
                elif n < IN0:
                    load_chunk(n, w_ik[:, n - IK0], 8 * IKW)
                else:
                    load_chunk(n, w_in[0, :, n - IN0])
                for _ in range(8):
                    if order:
                        load_ik(*order.pop(0))
            for dst, src in ((ln1_sb[:], ln1), (ln2_sb[:], ln2), (psc[:], pool_scale), (cnt[:], count_c)):
                sp.dma_start(dst, src).then_inc(late_in, 16)
            sp.wait_ge(ik_twice, 1)
            sp.dma_start(ikT_out, ik_d[0:ID, :]).then_inc(rows_out, 16)

            def load_k(j):
                if j == 0:
                    sp.wait_ge(s_sum, 10)
                    sp.wait_ge(wsel_kept, 2)
                    sp.wait_ge(iq_roped, 4)
                    sp.wait_ge(ik_roped, 1)
                if j >= KR:
                    sp.wait_ge(k_used, j - KR + 1)
                r = page_number(j)
                sp.dma_start(k_ring[:, j % KR, :],
                             kT_cache[bass.ds(r, 1)].rearrange("a p n -> p (a n)")).then_inc(k_in[j % KR], 16)

            def load_v(j):
                if j == 0:
                    wait_used(sp, OUT0 - 1)
                if j == VX:
                    sp.wait_ge(k_used, NPAGES)
                if j >= VR:
                    sp.wait_ge(v_used, j - VR + 1)
                slot = j % VR
                dst = v_ring_x[:, slot, :] if slot < VX else v_ring_k[:, slot - VX, :]
                r = page_number(j)
                sp.dma_start(dst, v_cache[bass.ds(r, 1)].rearrange("a p n -> p (a n)")).then_inc(v_in[slot], 16)

            for n in range(IN0 + 8, IN0 + 18):
                load_chunk(n, w_in[(n - IN0) // 8, :, (n - IN0) % 8])
            sp.wait_ge(p_relu, 24)
            sp.wait_ge(p_acc, 24)
            sp.wait_ge(iq_packed, 4)
            sp.dma_start(p_ext[:], pool_ctx).then_inc(ctx_in, 16)
            for j in range(KR):
                load_k(j)
            for s in range(2, 6):
                for c in range(2, 8):
                    load_chunk(IN0 + 8 * s + c, w_in[s, :, c])
                for c in range(2):
                    n = IN0 + 8 * (s + 1) + c
                    load_chunk(n, w_in[s + 1, :, c] if s < 5 else w_out[0, :, c])
                for j in range(KR + 32 * (s - 2), min(KR + 32 * (s - 1), NPAGES)):
                    load_k(j)
            sp.wait_ge(k_roped, 4)
            sp.dma_start(kT_out, k_t[:]).then_inc(rows_out, 16)
            sp.wait_ge(g_free, 4 * 5)
            sp.dma_start(vT_out, v_t[:]).then_inc(v_out, 16)
            sp.dma_start(wp_sb[:], w_pool).then_inc(pool_in, 16)
            sp.wait_ge(g_free, 4 * 7)
            sp.dma_start(pT_out, p_ext[:, :, P_OUT:P_EXT]).then_inc(rows_out, 16)
            load_chunk(OUT0 + 2, w_out[0, :, 2])
            for j in range(NPAGES):
                load_v(j)
            sp.wait_ge(v_used, NPAGES)
            sp.dma_start(z1[:], xT.rearrange("p (k t) -> p k t", t=T)).then_inc(x_again, 16)
            for c in range(3, 8):
                load_chunk(OUT0 + c, w_out[0, :, c])

            def steady(i, first, c, src):
                sp.wait_ge(lo_dve, i * 8 + (first + c - back(c) + 1 - LO_GAP))
                sp.dma_start(raw[:, c % RING, :], src).then_inc(raw_in[c % RING], 16)

            with sp.Fori(1, NOUT) as i:
                for c in range(8):
                    steady(i, OUT0, c, w_out[bass.ds(i, 1), :, c].rearrange("a p n -> p (a n)"))
            for c in range(RING):
                steady(0, UP0, c, w_up[0, :, c])
            sp.wait_ge(x1_lo, KB)
            sp.wait_ge(rows_out, 16 * 3)
            sp.wait_ge(v_out, 16)
            sp.dma_start(cp_sb[:], conv_p).then_inc(conv_in, 16)
            sp.dma_start(c_state[:], conv_ctx).then_inc(conv_in, 16)
            for c in range(RING, 8):
                steady(0, UP0, c, w_up[0, :, c])
            with sp.Fori(1, NUP) as i:
                for c in range(8):
                    steady(i, UP0, c, w_up[bass.ds(i, 1), :, c].rearrange("a p n -> p (a n)"))
            for n in range(DN0, DN0 + 8):
                load_chunk(n, w_down[0, :, n - DN0])
            sp.wait_ge(tail_put, 2 * NUP)
            sp.dma_start(cT_out, c_state[:]).then_inc(rows_out, 16)
            for n in range(DN0 + 8, END):
                load_chunk(n, w_down[(n - DN0) // DNC, :, (n - DN0) % DNC])
            for k in range(KB):
                sp.wait_ge(normed, KB + k + 1)
                sp.dma_start(yT[:, k], z2[:, k, :]).then_inc(rows_out, 16)
            sp.wait_ge(rows_out, 16 * (4 + KB))

        @block.tensor
        def _(pe):
            def three(out, hi, lo, xh, xl, start, stop):
                pe.matmul(out, hi, xh, start=start, stop=False)
                pe.matmul(out, hi, xl, start=False, stop=False)
                return pe.matmul(out, lo, xh, start=False, stop=stop)

            def chunk(c, rhs, k0, blocks, tile_free=None):
                for j in range(4):
                    if tile_free is not None:
                        tile_free(j)
                    for k in range(CK):
                        hi = w_hi[:, c % RING, CW * k + 128 * j:CW * k + 128 * j + 128]
                        lo = w_lo[:, c % RING, CW * k + 128 * j:CW * k + 128 * j + 128]
                        xh, xl = rhs(k0 + k)
                        mm = three(G[:, j, 0:T], hi, lo, xh, xl, k0 + k == 0, k0 + k == blocks - 1)
                    if k0 + CK == blocks and j < 3:
                        mm.then_inc(tile_done, 1)
                mm.then_inc(chunk_used, 1)

            def x_parts(k):
                return x_hi[:, k, :], x_lo[:, k, :]

            def slab(s, first):
                for c in range(8):
                    wait_lo(pe, first + c)
                    free = (lambda j: pe.wait_ge(g_free, 4 * (s - 1) + j + 1)) if c == 0 and s else None
                    chunk(c, x_parts, CK * c, KB, free)

            slab(0, IQ0)
            for c in range(2):
                wait_lo(pe, IK0 + c)
                for k in range(8):
                    hi, lo = w_hi[:, c, IKW * k:IKW * k + IKW], w_lo[:, c, IKW * k:IKW * k + IKW]
                    mm = three(A[0:IKW, 0, 0:T], hi, lo, *x_parts(8 * c + k), c + k == 0, c == 1 and k == 7)
                mm.then_inc(chunk_used, 1)
            slab(1, IN0)

            pe.wait_ge(consts_in, 96)
            pe.wait_ge(ik_kept, 2)
            for a, (t0, n) in enumerate(TOK[:3]):
                pe.transpose(A[0:n, 1, IH * a:IH * a + IH], iw_t[:, t0:t0 + n], ident[0:IH, 0:IH])
            pe.matmul(A[:, 1, 64:64 + TS], e8_sb[:], iw_t[:, TP:T], start=True, stop=True).then_inc(iw_turned, 1)

            pe.wait_ge(iq_packed, 4)
            pe.wait_ge(ik_twice, 1)

            def score_sum(e, c):
                pe.wait_ge(s_relu, 2 * e + 2)
                if e == 0:
                    pe.wait_ge(wsel_kept, 2)
                    pe.wait_ge(g_free, 8)
                for g in range(2):
                    mm = pe.matmul(G[0:TS, c, :], wsel[:, g, :], relu_s[:, e % 2, g, :],
                                   start=g == 0, stop=g == 1)
                    mm.then_inc(s_sum, 1)

            rounds = (0, 2, 1, 3)
            for e, c in enumerate(rounds):
                g2_, half = c % 2, c // 2
                pe.wait_ge(ik_in[g2_], 16 * DB * 8)
                if e == 0:
                    pe.wait_ge(wtok_kept, 2)
                    pe.wait_ge(wsel_kept, 2)
                if e >= 2:
                    pe.wait_ge(s_relu, 2 * e - 2)
                for g in range(2):
                    for m in range(4):
                        b = 4 * g + m
                        mm = pe.matmul(A[32 * m:32 * m + 32, 2 * (e % 2) + g, :],
                                       iq_s[64 * half:64 * half + 64, DQ * b:DQ * b + DQ, :],
                                       (ik_a, ik_b)[g2_][64 * half:64 * half + 64, b, :, :],
                                       start=True, stop=True)
                    mm.then_inc(s_raw, 1)
                if e:
                    score_sum(e - 1, rounds[e - 1])
            pe.wait_ge(s_relu, 6)
            for g in range(2):
                for m in range(4):
                    b = 4 * g + m
                    mm = pe.matmul(A[32 * m:32 * m + 32, 0, 32 * g:32 * g + 32],
                                   iq_s[0:64, DQ * b:DQ * b + DQ, :], ik_d[0:64, TP:T], start=True, stop=True)
            mm.then_inc(s_raw, 1)
            score_sum(3, rounds[3])
            pe.wait_ge(s_relu, 9)
            pe.wait_ge(s_kept, 1)
            for g in range(2):
                mm = pe.matmul(G[0:TS, 0, 0:TS], wsel[:, g, :], relu_s[:, 0, g, 0:TS], start=g == 0, stop=g == 1)
                mm.then_inc(s_sum, 1)

            pe.wait_ge(iq_roped, 4)
            for u in range(24):
                i, h = u // IH, u % IH
                t0, n, keys, _ = PQ[i]
                if u >= 4:
                    pe.wait_ge(p_relu, u - 3)
                else:
                    pe.wait_ge(s_relu, 9)
                o = 64 * (h % 2)
                pe.matmul(A[0:n, u % 4, 0:keys], iq_t[o:o + 64, h // 2, t0:t0 + n], ik_d[o:o + 64, 0:keys],
                          start=True, stop=True).then_inc(p_raw, 1)

            pe.wait_ge(s_kept, 5)
            slab(2, IN0 + 8)

            def sample_scores(b):
                if b == 0:
                    pe.wait_ge(q_roped, NH)
                    pe.wait_ge(p_relu, 24)
                if b >= 2:
                    pe.wait_ge(qk_kept, b - 1)
                for g in range(NPG):
                    j = NPG * b + g
                    pe.wait_ge(k_in[j % KR], 16 * (j // KR + 1))
                    for h in range(KVH):
                        mm = pe.matmul(A[:, b % 2, 32 * g + 8 * h:32 * g + 8 * h + 8],
                                       k_ring[:, j % KR, 128 * h:128 * h + 128],
                                       q_t[:, 2 * h:2 * h + 2, TP + DQ * b:TP + DQ * b + DQ], start=True, stop=True)
                    mm.then_inc(k_used, 1)

            slab(3, IN0 + 16)
            sample_scores(0)
            sample_scores(1)
            slab(4, IN0 + 24)
            pe.wait_ge(k_roped, KVH)
            for h in range(KVH):
                mm = pe.matmul(A[0:TS, 2, 64 * h:64 * h + 64], k_t[:, h, TP:T], q_t[:, 2 * h:2 * h + 2, TP:T],
                               start=True, stop=True)
            mm.then_inc(new_done, 1)
            sample_scores(2)
            sample_scores(3)
            slab(5, IN0 + 32)
            pe.wait_ge(new_kept, 1)
            for a, (t0, n) in enumerate(TOK):
                if a >= 2:
                    pe.wait_ge(v_kept, a - 1)
                for h in range(KVH):
                    mm = pe.transpose(A[0:n, 2 + a % 2, 128 * h:128 * h + 128], v_t[:, h, t0:t0 + n], ident[:])
                mm.then_inc(v_turned, 1)
            sample_scores(4)
            sample_scores(5)
            slab(6, IN0 + 40)
            sample_scores(6)
            sample_scores(7)

            def prompt_scores(n):
                if n == 0:
                    pe.wait_ge(mask_kept, 3)
                    pe.wait_ge(v_kept, 4)
                if n >= 2:
                    pe.wait_ge(pa_m, 3 * (n - 1))
                a = 2 * (n % 2)
                for i, out in enumerate((A[:, a, 0:128], A[:, a + 1, 0:256], A[0:16, a, 128:400])):
                    t0, rows, keys, _ = PQ[i]
                    pe.matmul(out, q_t[:, n, t0:t0 + rows], k_t[:, n // 2, 0:keys],
                              start=True, stop=True).then_inc(pa_s, 1)

            def prompt_apply(n):
                for i in range(3):
                    t0, rows, keys, _ = PQ[i]
                    pe.wait_ge(pa_n, 3 * n + i + 1)
                    if n and i == 0:
                        pe.wait_ge(pa_tk, 3 * n)
                    for kt in range(i + 1):
                        kn = min(128, keys - 128 * kt)
                        out = G[0:kn, kt, t0:t0 + rows] if kt < 2 else G[0:kn, 1, 400:400 + rows]
                        mm = pe.transpose(out, prob[0:rows, i, 128 * kt:128 * kt + kn], ident[0:rows, 0:rows])
                    mm.then_inc(pa_t, 1)
                pe.wait_ge(pa_tk, 3 * n + 3)
                if n >= 2:
                    pe.wait_ge(pa_lo, n - 1)
                out = G[:, 2 + n % 2, 0:TP]
                h = 128 * (n // 2)
                pe.matmul(out, v_tok[:, 0, h:h + 128], prob_t[:, 0, :], start=True, stop=False)
                pe.matmul(out[:, 128:TP], v_tok[:, 1, h:h + 128], prob_t[:, 1, 128:TP], start=False, stop=False)
                pe.matmul(out[:, 256:TP], v_tok[0:16, 2, h:h + 128], prob_t[0:16, 2, 256:TP],
                          start=False, stop=True).then_inc(pa_o, 1)

            pe.wait_ge(qk_kept, DB)
            pe.wait_ge(s_masked, 1)
            for g in range(NPG):
                pe.transpose(A[:, 0, TS * g:TS * g + TS], score[:, PAGE * g:PAGE * g + PAGE], ident[0:TS, 0:TS])
            pe.transpose(A[0:TS, 1, 0:TS], score[:, PAST:PAST + TS], ident[0:TS, 0:TS]).then_inc(mask_t, 1)
            pe.wait_ge(pool_in, 16)
            for g in range(4):
                pe.wait_ge(windowed, 2 * g + 2)
                if g == 0:
                    pe.wait_ge(g_free, 4 * 7)
                if g >= 2:
                    pe.wait_ge(m_split, 2 * g - 2)
                for e in range(2):
                    for c in range(2):
                        mm = pe.matmul(G[:, 2 * (g % 2) + e, 0:T], wp_sb[:, g, c, 128 * e:128 * e + 128],
                                       pooled[:, 2 * g + c, :], start=c == 0, stop=c == 1)
                    mm.then_inc(pool_mm, 1)
            pe.wait_ge(m_split, 8)
            for n in range(NH + 1):
                if n < NH:
                    prompt_scores(n)
                if n:
                    prompt_apply(n - 1)

            pe.wait_ge(max_col, DB)
            pe.wait_ge(pa_m, 3 * NH)
            pe.wait_ge(preset, 1)
            for a in range(2):
                mm = pe.transpose(A[:, 2, 128 * a:128 * a + 128], smax[:, 128 * a:128 * a + 128], ident[:])
            mm.then_inc(max_t, 1)
            pe.wait_ge(max_diag, 2)
            for a in range(2):
                mm = pe.matmul(A[:, 3, 128 * a:128 * a + 128], ones[:], prob_t[:, a, 0:128], start=True, stop=True)
            mm.then_inc(max_all, 1)
            pe.wait_ge(mask_kept, 3)
            for b in range(DB):
                pe.wait_ge(s_exp, b + 1)
                for h in range(KVH):
                    pe.matmul(A[:, 0, 32 * b + 8 * h:32 * b + 8 * h + 8], v_tok[0:TS, 3, 128 * h:128 * h + 128],
                              s_buf[0:TS, b, 512 + 8 * h:520 + 8 * h], start=h == 0, stop=False,
                              skip_group_check=True)
                for g in range(NPG):
                    j = NPG * b + g
                    slot = j % VR
                    pe.wait_ge(v_in[slot], 16 * (j // VR + 1))
                    page = v_ring_x[:, slot, :] if slot < VX else v_ring_k[:, slot - VX, :]
                    for h in range(KVH):
                        mm = pe.matmul(A[:, 0, 32 * b + 8 * h:32 * b + 8 * h + 8], page[:, 128 * h:128 * h + 128],
                                       s_buf[:, b, 32 * g + 8 * h:32 * g + 8 * h + 8],
                                       start=False, stop=g == NPG - 1, skip_group_check=True)
                    mm.then_inc(v_used, 1)
            pe.wait_ge(s_colsum, DB)
            pe.matmul(A[:, 3, 256:512], ones[:], smax[:], start=True, stop=True).then_inc(s_den, 1)

            def mix_parts(k):
                return (a_hi[:, k], a_lo[:, k]) if k < 8 else (m_hi[:, k - 8], m_lo[:, k - 8])

            pe.wait_ge(pa_lo, NH)
            pe.wait_ge(sa_lo, 1)
            pe.wait_ge(m_split, 8)
            with pe.Fori(0, NOUT) as i:
                for c in range(8):
                    pe.wait_ge(lo_dve, i * 8 + (OUT0 + c + 1 - LO_GAP))
                    free = (lambda j: pe.wait_ge(g_free, i * 4 + (4 * (SLAB_OUT - 1) + j + 1))) if c == 0 else None
                    chunk(c, mix_parts, CK * c, KB, free)

            def norm(z, tmp, done, round_):
                for k in range(KB):
                    pe.wait_ge(g_free, done + k + 1)
                    mm = pe.matmul(A[:, 1, 0:T], ones[:], z[:, k, :], start=k == 0, stop=k == KB - 1)
                mm.then_inc(mean_mm, 1)
                for k in range(KB):
                    pe.wait_ge(squared, KB * round_ + k + 1)
                    mm = pe.matmul(A[:, 2, 0:T], ones[:], tmp[:, 2 + k % 2, :], start=k == 0, stop=k == KB - 1)
                    mm.then_inc(var_mm, 1)

            norm(z1, ln_a, 4 * SLAB_OUT, 0)

            pe.wait_ge(x1_lo, KB)
            with pe.Fori(0, NUP) as i:
                for c in range(8):
                    pe.wait_ge(lo_dve, i * 8 + (UP0 + c + 1 - LO_GAP))
                    free = (lambda j: pe.wait_ge(g_free, i * 4 + (4 * (SLAB_UP - 1) + j + 1))) if c == 0 else None
                    chunk(c, x_parts, CK * c, KB, free)

            with pe.Fori(0, NDN // 2) as i:
                for s in range(2):
                    for c in range(DNC):
                        cc = DNC * s + c
                        pe.wait_ge(lo_dve, i * 2 * DNC + (DN0 + cc + 1 - LO_GAP))
                        if s == 0 and c == (2 * NUP - 2) // CK:
                            pe.wait_ge(h_split, 2 * NUP)
                        free = (lambda j: pe.wait_ge(g_free, i * 8 + (4 * (SLAB_DN - 1 + s) + j + 1))) \
                            if c == 0 else None
                        if s == 0 and c == 0:
                            pe.wait_ge(h_split, 2 * NUP - 2)
                        chunk(cc, lambda k: (h_hi[:, k], h_lo[:, k]), CK * c, FB, free)
            norm(z2, ln_b, 4 * SLAB_DN, 1)

        @block.gpsimd
        def _(pool):
            pool.memset(ones[:], 1.0).then_inc(preset, 1)
            pool.memset(tiny[:, 15:16], EPS).then_inc(preset, 1)
            for i, (t0, n, keys, col) in enumerate(PQ):
                pool.wait_ge(p_acc, 8 * i + 8)
                view = p_score[0:n, col:col + keys]
                pool.affine_select(out=view, in_=view, pattern=[[-1, keys]], compare_op=ALU.is_ge, fill=NEG,
                                   base=t0, channel_multiplier=1).then_inc(p_causal, 1)
            pool.wait_ge(s_raw, 8)
            pool.memset(s_buf[:, :, 512:544], 0.0).then_inc(preset, 1)
            for n in range(*POOL_LO):
                pool.wait_ge(hi_done, n + 1)
                c = position(n) % RING
                pool.tensor_tensor(w_lo[:, c], raw[:, c], w_hi[:, c].bitcast(f32), ALU.subtract).then_inc(lo_pool, 1)
            pool.wait_ge(x1_lo, KB)
            pool.wait_ge(rows_out, 48)
            pool.wait_ge(v_out, 16)
            pool.memset(u_ext[:], 0.0).then_inc(preset, 1)
            pool.wait_ge(preset, 4)
            pool.wait_ge(conv_in, 32)
            with pool.Fori(0, NUP) as i:
                for a in range(2):
                    pool.wait_ge(conv_v, i * 4)
                    pool.wait_ge(conv_in, 32)
                    src = c_state[:, bass.ds(2 * i + FB * a, 2), 0:16].rearrange("p j (b w) -> p j b w", w=2)
                    dst = u_ext[:, 2 * a:2 * a + 2, US0:US0 + 6 * DB].rearrange("p j (b w) -> p j b w", w=6)
                    pool.tensor_copy(dst[:, :, :, 0:2], src).then_inc(ctx_put, 1)
                flat = c_state[:].rearrange("p j w -> p (j w)")
                for a in range(2):
                    pool.wait_ge(g_free, i * 4 + (4 * SLAB_UP + 2 * a + 2))
                    pool.wait_ge(ctx_put, i * 2 + 2)
                    dst = flat[:, bass.ds(i * 36 + 18 * FB * a, 36)].rearrange("p (j b w) -> p j b w", b=9, w=2)
                    src = u_ext[:, 2 * a:2 * a + 2, TP:TP + 54].rearrange("p j (b w) -> p j b w", w=6)
                    pool.tensor_copy(dst, src[:, :, :, 0:2]).then_inc(tail_put, 1)
            pool.wait_ge(h_split, 2 * NUP)
            pool.wait_ge(tail_put, 2 * NUP)
            for k in range(KB):
                pool.tensor_tensor(z2[:, k], x_hi[:, k].bitcast(f32), x_lo[:, k].bitcast(f32),
                                   ALU.add).then_inc(residual, 1)

        @block.scalar
        def _(act):
            def hi(n, width=CK * CW):
                c = position(n)
                act.wait_ge(raw_in[c % RING], 16 * loads(n))
                if n < NX:
                    act.activation(x_hi[:, CK * n:CK * n + CK].rearrange("p k t -> p (k t)"),
                                   raw[:, c % RING, 0:CK * T], ACT.Copy).then_inc(hi_done, 1)
                    return
                wait_used(act, n - back(c))
                act.activation(w_hi[:, c % RING, 0:width], raw[:, c % RING, 0:width], ACT.Copy).then_inc(hi_done, 1)

            def hi_loop(i, n):
                c = position(n)
                act.wait_ge(raw_in[c % RING], i * (16 * per_slab(c)) + 16 * loads(n))
                act.wait_ge(chunk_used, i * 8 + (n - back(c) + 1 - IQ0))
                act.activation(w_hi[:, c % RING, :], raw[:, c % RING, :], ACT.Copy).then_inc(hi_done, 1)

            for n in range(IK0):
                hi(n)
            hi(IK0, 8 * IKW)
            hi(IK0 + 1, 8 * IKW)
            for j in range(4):
                wait_tile(act, 0, j)
                act.activation(iq_t[:, j], G[:, j, 0:T], ACT.Copy).then_inc(g_free, 1)
            hi(IN0)
            wait_used(act, IN0 - 1)
            act.activation(ik_d[0:ID, :], A[0:ID, 0, 0:T], ACT.Copy).then_inc(ik_kept, 1)
            act.activation(iw_t[:], A[ID:IKW, 0, 0:T], ACT.Copy).then_inc(ik_kept, 1)
            hi(IN0 + 1)
            hi(IN0 + 2)
            act.wait_ge(ik_roped, 1)
            act.activation(ik_d[64:128, :], ik_d[0:64, :], ACT.Copy).then_inc(ik_twice, 1)
            for c in range(3, 8):
                hi(IN0 + c)
            act.wait_ge(iq_roped, 4)
            for half in range(2):
                for odd in range(2):
                    act.activation(iq_s[64 * half:64 * half + 64].rearrange("p t (m o) -> p m t o", o=2)[:, :, :, odd],
                                   iq_t[64 * odd:64 * odd + 64, :, TP:T], ACT.Copy).then_inc(iq_packed, 1)
            for c in range(2):
                hi(IN0 + 8 + c)

            def keep_q(s):
                for j in range(4):
                    wait_tile(act, s, j)
                    act.activation(q_t[:, 4 * (s - 1) + j], G[:, j, 0:T], ACT.Copy).then_inc(g_free, 1)

            keep_q(1)
            act.wait_ge(iw_turned, 1)
            w_scale = float(np.float32(IH ** -0.5)) * ID ** -0.5
            act.activation(wtok[:, 0:2].rearrange("p a h -> p (a h)"), A[:, 1, 0:16], ACT.Copy,
                           scale=w_scale).then_inc(wtok_kept, 1)
            act.activation(wtok[0:16, 2], A[0:16, 1, 16:24], ACT.Copy, scale=w_scale).then_inc(wtok_kept, 1)
            for e in range(4):
                for g in range(2):
                    act.wait_ge(s_raw, 2 * e + g + 1)
                    if e >= 2:
                        act.wait_ge(s_sum, 2 * e - 2)
                    act.activation(relu_s[:, e % 2, g, :], A[:, 2 * (e % 2) + g, :], ACT.Relu).then_inc(s_relu, 1)
            act.wait_ge(s_raw, 9)
            act.wait_ge(s_sum, 6)
            act.activation(relu_s[:, 0, :, 0:32], A[:, 0, 0:64].rearrange("p (g t) -> p g t", g=2),
                           ACT.Relu).then_inc(s_relu, 1)
            for u in range(24):
                _, n, keys, _ = PQ[u // IH]
                act.wait_ge(p_raw, u + 1)
                if u >= 4:
                    act.wait_ge(p_acc, u - 3)
                act.activation(relu_p[0:n, u % 4, 0:keys], A[0:n, u % 4, 0:keys], ACT.Relu).then_inc(p_relu, 1)
            for c in range(2, 8):
                hi(IN0 + 8 + c)

            def next_two(n):
                hi(n)
                hi(n + 1)

            def keep_scores(b):
                if b == 0:
                    act.wait_ge(s_relu, 9)
                act.wait_ge(k_used, NPG * (b + 1))
                act.activation(s_buf[:, b, 0:512], A[:, b % 2, :], ACT.Copy).then_inc(qk_kept, 1)

            next_two(IN0 + 16)
            keep_q(2)
            for c in range(2, 8):
                hi(IN0 + 16 + c)
            next_two(IN0 + 24)
            for j in range(4):
                wait_tile(act, 3, j)
                act.activation(k_t[:, j], G[:, j, 0:T], ACT.Copy).then_inc(g_free, 1)
            keep_scores(0)
            hi(IN0 + 26)
            keep_scores(1)
            for c in range(3, 8):
                hi(IN0 + 24 + c)
            next_two(IN0 + 32)
            act.wait_ge(q_roped, NH)
            for j in range(4):
                wait_tile(act, 4, j)
                act.activation(v_t[:, j], G[:, j, 0:T], ACT.Copy).then_inc(g_free, 1)
            act.wait_ge(new_done, 1)
            act.wait_ge(preset, 3)
            for h in range(KVH):
                for r in range(2):
                    o = 512 + 8 * h + 4 * r
                    ins = act.activation(s_buf[0:TS, :, o:o + 4],
                                         A[0:TS, 2, 64 * h + 32 * r:64 * h + 32 * r + 32]
                                         .rearrange("p (b q) -> p b q", q=DQ), ACT.Copy)
            ins.then_inc(new_kept, 1)
            keep_scores(2)
            hi(IN0 + 34)
            keep_scores(3)
            for c in range(3, 8):
                hi(IN0 + 32 + c)
            next_two(IN0 + 40)

            def keep_p(s, m0):
                for j in range(4):
                    wait_tile(act, s, j)
                    if s == 5 and j == 0:
                        act.wait_ge(ctx_in, 16)
                    act.activation(p_ext[:, m0 + j, CTX:CTX + TP], G[:, j, 0:TP], ACT.Copy).then_inc(act_own, 1)
                    act.activation(samples(p_ext[:, m0 + j, PS0:P_EXT], CTX + DQ, CTX, DQ),
                                   G[:, j, TP:T].rearrange("p (b q) -> p b q", q=DQ), ACT.Copy).then_inc(g_free, 1)

            keep_p(5, 0)
            for a, (t0, n) in enumerate(TOK):
                act.wait_ge(v_turned, a + 1)
                act.activation(v_tok[0:n, a, :], A[0:n, 2 + a % 2, :], ACT.Copy).then_inc(v_kept, 1)
            keep_scores(4)
            hi(IN0 + 42)
            keep_scores(5)
            for c in range(3, 8):
                hi(IN0 + 40 + c)
            next_two(OUT0)
            keep_p(6, 4)
            keep_scores(6)
            hi(OUT0 + 2)
            keep_scores(7)

            act.wait_ge(late_in, 64)
            act.wait_ge(mask_t, 1)
            for m in range(8):
                act.wait_ge(pool_mm, m + 1)
                act.activation(m_hi[:, m], G[:, m % 4, 0:T], ACT.Copy, scale=psc[:, m:m + 1]).then_inc(m_high, 1)

            for n in range(NH):
                for i, (t0, rows, keys, _) in enumerate(PQ):
                    act.wait_ge(pa_m, 3 * n + i + 1)
                    act.activation(prob[0:rows, i, 0:keys], prob[0:rows, i, 0:keys], ACT.Exp,
                                   bias=tiny[0:rows, 3 + i:4 + i], scale=SCALE,
                                   accum_out=tiny[0:rows, 6 + i:7 + i]).then_inc(pa_e, 1)
                if n:
                    act.wait_ge(pa_o, n)
                act.wait_ge(pa_t, 3 * n + 3)
                for i in range(3):
                    if i == 0:
                        act.activation(prob_t[:, 0, 0:128], G[:, 0, 0:128], ACT.Copy).then_inc(pa_tk, 1)
                    elif i == 1:
                        act.activation(prob_t[:, 0:2, 128:256], G[:, 0:2, 128:256], ACT.Copy).then_inc(pa_tk, 1)
                    else:
                        act.activation(prob_t[:, 0:2, 256:TP], G[:, 0:2, 256:TP], ACT.Copy).then_inc(act_own, 1)
                        act.activation(prob_t[0:16, 2, 256:TP], G[0:16, 1, 400:416], ACT.Copy).then_inc(pa_tk, 1)
                act.wait_ge(pa_o, n + 1)
                act.activation(a_hi[:, n, 0:TP], G[:, 2 + n % 2, 0:TP], ACT.Copy).then_inc(pa_hi, 1)

            for b in range(DB):
                act.wait_ge(s_shift, b + 1)
                act.activation(s_buf[:, b], s_buf[:, b], ACT.Exp, scale=SCALE).then_inc(s_exp, 1)
            act.wait_ge(sa_n, 1)
            act.activation(a_hi[:, :, TP:T].rearrange("p m (b q) -> p m b q", q=DQ),
                           win[:, 1, 0:256].rearrange("p (b m q) -> p m b q", m=NH, q=DQ),
                           ACT.Copy).then_inc(sa_hi, 1)

            for n in range(OUT0 + 3, UP0 + RING):
                hi(n)

            def norm(z, tmp, round_, split):
                par = (ln1_sb, ln2_sb)[round_]
                for k in range(KB):
                    act.wait_ge(centred, KB * round_ + k + 1)
                    if k >= 2:
                        act.wait_ge(var_mm, KB * round_ + k - 1)
                    act.activation(tmp[:, 2 + k % 2], z[:, k], ACT.Square).then_inc(squared, 1)
                act.wait_ge(var_mm, KB * (round_ + 1))
                act.activation(tmp[:, 1], A[:, 2, 0:T], ACT.Sqrt, bias=tiny[:, 15:16],
                               scale=1.0 / D).then_inc(sd_done, 1)
                for k in range(KB):
                    act.wait_ge(scaled, KB * round_ + k + 1)
                    act.activation(z[:, k], z[:, k], ACT.Identity, scale=par[:, 0, k:k + 1],
                                   bias=par[:, 1, k:k + 1]).then_inc(normed, 1)
                    if split:
                        act.wait_ge(normed, KB * round_ + k + 1)
                        act.activation(x_hi[:, k], z[:, k], ACT.Copy).then_inc(x1_hi, 1)

            act.wait_ge(late_in, 64)
            norm(z1, ln_a, 0, True)

            for n in range(UP0 + RING, UP0 + 6):
                hi(n)
            act.wait_ge(conv_in, 32)
            act.wait_ge(preset, 4)
            with act.Fori(0, NUP) as i:
                for n in range(UP0 + 6, UP0 + 10):
                    hi_loop(i, n)
                for j in range(4):
                    if j < 3:
                        act.wait_ge(tile_done, i * 3 + (3 * SLAB_UP + j + 1))
                    else:
                        act.wait_ge(chunk_used, i * 8 + (UP0 + 8 - IQ0))
                    act.wait_ge(conv_v, i * 4)
                    act.wait_ge(tail_put, i * 2)
                    act.activation(u_ext[:, j, 2:US0], G[:, j, 0:TP], ACT.Copy).then_inc(act_own, 1)
                    act.activation(samples(u_ext[:, j, US0:US0 + 6 * DB], 2 + DQ, 2, DQ),
                                   G[:, j, TP:T].rearrange("p (b q) -> p b q", q=DQ), ACT.Copy).then_inc(g_free, 1)
                for n in range(UP0 + 10, UP0 + 14):
                    for j in {UP0 + 10: (0, 1), UP0 + 11: (2, 3)}.get(n, ()):
                        act.wait_ge(ctx_put, i * 2 + (1 + j // 2))
                        act.wait_ge(act_own, i * 4 + (8 + NH + j + 1))
                        act.wait_ge(g_free, i * 4 + (4 * SLAB_UP + j + 1))
                        act.wait_ge(gated_done, i)
                        act.wait_ge(consts_in, 96)
                        t = bass.ds(2 * i + (j % 2 + FB * (j // 2)), 1)
                        act.activation(conv[:, j, 0:UO], u_ext[:, j, 0:UO], ACT.Identity,
                                       scale=cp_sb[:, t, 0:1].rearrange("p a w -> p (a w)"),
                                       bias=cp_sb[:, t, 3:4].rearrange("p a w -> p (a w)")).then_inc(conv_a, 1)
                    if n == UP0 + 12:
                        act.wait_ge(conv_v, i * 4 + 2)
                        act.activation(conv[:, 0:2, 0:UO], conv[:, 0:2, 0:UO], ACT.Silu).then_inc(silu_done, 1)
                    if n == UP0 + 13:
                        act.wait_ge(gated_done, i + 1)
                        act.wait_ge(consts_in, 96)
                        act.activation(h_hi[:, bass.ds(2 * i, 2), 0:TP], gated[:, :, 0:TP], ACT.Copy).then_inc(h_high, 1)
                        act.activation(h_hi[:, bass.ds(2 * i, 2), TP:T].rearrange("p j (b q) -> p j b q", q=DQ),
                                       gated[:, :, US0:US0 + 6 * DB].rearrange("p j (b q) -> p j b q", q=6)[:, :, :, 0:DQ],
                                       ACT.Copy).then_inc(h_high, 1)
                    hi_loop(i, n)
            for n in range(DN0 + 6, END):
                hi(n)
            norm(z2, ln_b, 1, False)

        @block.vector
        def _(dve):
            own = [0]

            def then(ins):
                own[0] += 1
                ins.then_inc(dve_own, 1)
                dve.wait_ge(dve_own, own[0])

            def lo(n):
                c = position(n) % RING
                dve.wait_ge(hi_done, n + 1)
                if n < NX:
                    dve.tensor_tensor(x_lo[:, CK * n:CK * n + CK].rearrange("p k t -> p (k t)"), raw[:, c, 0:CK * T],
                                      x_hi[:, CK * n:CK * n + CK].rearrange("p k t -> p (k t)").bitcast(f32),
                                      ALU.subtract).then_inc(lo_dve, 1)
                else:
                    width = 8 * IKW if IK0 <= n < IN0 else CK * CW
                    dve.tensor_tensor(w_lo[:, c, 0:width], raw[:, c, 0:width], w_hi[:, c, 0:width].bitcast(f32),
                                      ALU.subtract).then_inc(lo_dve, 1)

            def rope(x, table, mask, done):
                p = x.shape[0]
                then(dve.stream_shuffle(swap[0:p], x, mask))
                then(dve.tensor_tensor(swap[0:p], swap[0:p], table[0:p, 1], ALU.mult))
                then(dve.tensor_tensor(x, x, table[0:p, 0], ALU.mult))
                dve.tensor_tensor(x, x, swap[0:p], ALU.add).then_inc(done, 1)

            partner_i = [r + 8 if r < 8 else r - 8 if r < 16 else r for r in range(32)]
            partner_q = [(r + 16) % 32 for r in range(32)]

            for n in range(IN0 + 2):
                lo(n)
            dve.wait_ge(consts_in, 96)
            dve.wait_ge(ik_kept, 1)
            rope(ik_d[0:64], rope_i, partner_i, ik_roped)
            lo(IN0 + 2)
            for j in range(4):
                dve.wait_ge(ik_roped if j == 0 else iq_roped, max(j, 1))
                dve.wait_ge(g_free, j + 1)
                rope(iq_t[:, j], rope_i, partner_i, iq_roped)
                lo(IN0 + 3 + j)
            lo(IN0 + 7)

            dve.wait_ge(iw_turned, 1)
            dve.wait_ge(wtok_kept, 2)
            for g in range(2):
                dve.tensor_tensor(wsel[:, g], A[:, 1, 64:64 + TS], sel_sb[:, g], ALU.mult).then_inc(wsel_kept, 1)
            for e, c in enumerate((0, 2, 1, 3)):
                dve.wait_ge(s_sum, 2 * e + 2)
                dve.tensor_copy(score[:, 512 * c:512 * c + 512], G[0:TS, c, :]).then_inc(s_kept, 1)
            dve.wait_ge(s_sum, 10)
            then(dve.tensor_tensor(score[:, PAST:PAST + TS], G[0:TS, 0, 0:TS], new_sb[:, 0], ALU.mult))
            dve.tensor_tensor(score[:, PAST:PAST + TS], score[:, PAST:PAST + TS], new_sb[:, 1],
                              ALU.add).then_inc(s_kept, 1)

            dve.wait_ge(wtok_kept, 2)
            for u in range(24):
                i, h = u // IH, u % IH
                _, n, keys, col = PQ[i]
                view, part, w = p_score[0:n, col:col + keys], relu_p[0:n, u % 4, 0:keys], wtok[0:n, i, h:h + 1]
                dve.wait_ge(p_relu, u + 1)
                if h == 0:
                    dve.tensor_scalar(view, part, w, None, ALU.mult).then_inc(p_acc, 1)
                else:
                    dve.wait_ge(p_acc, u)
                    dve.scalar_tensor_tensor(out=view, in0=part, scalar=w, in1=view, op0=ALU.mult,
                                             op1=ALU.add).then_inc(p_acc, 1)

            def rope_heads(x, heads, done, kept):
                for j in heads:
                    if j:
                        dve.wait_ge(done, j)
                    dve.wait_ge(g_free, kept + j + 1)
                    rope(x[0:32, j], rope_q, partner_q, done)

            def top_rounds(src, buf, rounds, first, last):
                for r in rounds:
                    then(dve.max(top8[0:src.shape[0]], src if r == first else buf))
                    if r != last:
                        then(dve.match_replace(buf, top8[0:src.shape[0]], src if r == first else buf, NEG))

            def top_mask(src, buf, k, step):
                p, width = src.shape
                c = tiny[0:p, :]
                then(dve.tensor_scalar(buf, src, top8[0:p, 7:8], 0.0, ALU.is_gt, ALU.add, accum_out=c[:, 0:1]))
                then(dve.tensor_scalar(c[:, 1:2], c[:, 0:1], -1.0, float(k), ALU.mult, ALU.add))
                then(dve.tensor_scalar(c[:, 2:3], top8[0:p, 7:8], 0.5 * NEG, None, ALU.max))
                then(dve.tensor_scalar(src, src, c[:, 2:3], None, ALU.is_equal))
                for n, o in enumerate(range(0, width, step)):
                    m = min(step, width - o)
                    cs = win[0:p, n % 2, 0:m]
                    start = win[0:p, (n + 1) % 2, step - 1:step] if n else 0.0
                    then(dve.tensor_tensor_scan(cs, src[:, o:o + m], src[:, o:o + m], start, ALU.add, ALU.max))
                    then(dve.scalar_tensor_tensor(out=src[:, o:o + m], in0=cs, scalar=c[:, 1:2], in1=src[:, o:o + m],
                                                  op0=ALU.is_le, op1=ALU.mult))

            dve.wait_ge(iq_roped, 4)
            rope_heads(q_t, range(4), q_roped, 4)
            for i, (_, n, keys, col) in enumerate(PQ):
                dve.wait_ge(p_causal, i + 1)
                dve.wait_ge(q_roped, 4)
                src, buf = p_score[0:n, col:col + keys], p_work[0:n, col:col + keys]
                last = TOPK_P // 8 - 1
                top_rounds(src, buf, range(last + 1), 0, last)
                top_mask(src, buf, TOPK_P, keys)
                then(dve.tensor_tensor(src, src, buf, ALU.add))
                then(dve.tensor_scalar(src, src, FAR, -FAR, ALU.mult, ALU.add))
            rope_heads(q_t, range(4, 8), q_roped, 4)

            last = TOPK_S // 8 - 1
            dve.wait_ge(s_kept, 5)
            top_rounds(score[:], work[:], range(0, 4), 0, last)
            dve.wait_ge(q_roped, NH)
            rope_heads(k_t, range(4), k_roped, 12)
            top_rounds(score[:], work[:], range(4, 16), 0, last)

            def windows(m):
                w = WINS[m // 2]
                dve.wait_ge(act_own, m + 1)
                dve.wait_ge(g_free, 4 * 5 + m + 1)
                x, a = p_ext[:, m], p_ext[:, m]
                for lv in range(m // 2 + 1):
                    s, b = 2 ** lv, 2 ** (lv + 1) - 1
                    then(dve.tensor_tensor(win[:, lv % 2, b:P_EXT], a[:, b:P_EXT], a[:, b - s:P_EXT - s], ALU.add))
                    a = win[:, lv % 2]
                o = win[:, (lv + 1) % 2, 0:16]
                then(dve.tensor_tensor(o, a[:, CTX:CTX + 16], cnt[:, m // 2], ALU.mult))
                then(dve.scalar_tensor_tensor(out=pooled[:, m, 16:TP], in0=a[:, CTX + 16:CTX + TP], scalar=1.0 / w,
                                              in1=x[:, CTX + 16:CTX + TP], op0=ALU.mult, op1=ALU.subtract))
                then(dve.tensor_tensor(pooled[:, m, 0:16], o, x[:, CTX:CTX + 16], ALU.subtract))
                dve.scalar_tensor_tensor(out=pooled[:, m, TP:T].rearrange("p (b q) -> p b q", q=DQ),
                                         in0=samples(a[:, PS0:P_EXT], CTX + DQ, CTX, DQ), scalar=1.0 / w,
                                         in1=samples(x[:, PS0:P_EXT], CTX + DQ, CTX, DQ),
                                         op0=ALU.mult, op1=ALU.subtract).then_inc(windowed, 1)
                dve.wait_ge(windowed, m + 1)

            dve.wait_ge(late_in, 64)
            dve.wait_ge(k_roped, KVH)
            for m in range(4):
                windows(m)
            top_rounds(score[:], work[:], range(16, last + 1), 0, last)
            top_mask(score[:], work[:], TOPK_S, 416)
            dve.tensor_tensor(score[:], score[:], work[:], ALU.add).then_inc(s_masked, 1)
            for m in range(4, 8):
                windows(m)

            dve.wait_ge(mask_t, 1)
            wait_used(dve, OUT0 - 1)
            dve.memset(mask_s[:, NPG], -FAR).then_inc(mask_kept, 1)
            dve.tensor_scalar(mask_s[:, 0:NPG].rearrange("p g t -> p (g t)"), A[:, 0, :], FAR, -FAR,
                              ALU.mult, ALU.add).then_inc(mask_kept, 1)
            dve.wait_ge(mask_kept, 2)
            dve.tensor_scalar(mask_s[0:TS, NPG], A[0:TS, 1, 0:TS], FAR, -FAR, ALU.mult, ALU.add).then_inc(mask_kept, 1)

            for m in range(8):
                dve.wait_ge(m_high, m + 1)
                dve.scalar_tensor_tensor(out=m_lo[:, m], in0=G[:, m % 4, 0:T], scalar=psc[:, m:m + 1],
                                         in1=m_hi[:, m].bitcast(f32), op0=ALU.mult, op1=ALU.subtract).then_inc(m_split, 1)

            dve.wait_ge(v_out, 16)
            dve.wait_ge(v_turned, 4)
            for n in range(NH):
                a = 2 * (n % 2)
                banks = (A[:, a, 0:128], A[:, a + 1, 0:256], A[0:16, a, 128:400])
                dve.wait_ge(pa_s, 3 * n + 3)
                for i, (t0, rows, keys, col) in enumerate(PQ):
                    if n:
                        dve.wait_ge(pa_t, 3 * (n - 1) + i + 1)
                    then(dve.tensor_tensor_reduce(prob[0:rows, i, 0:keys], banks[i], p_score[0:rows, col:col + keys],
                                                  1.0, NEG, ALU.add, ALU.max, tiny[0:rows, i:i + 1]))
                    dve.tensor_scalar(tiny[0:rows, 3 + i:4 + i], tiny[0:rows, i:i + 1], -SCALE, None,
                                      ALU.mult).then_inc(pa_m, 1)
                for i, (t0, rows, keys, col) in enumerate(PQ):
                    dve.wait_ge(pa_e, 3 * n + i + 1)
                    then(dve.reciprocal(tiny[0:rows, 9 + i:10 + i], tiny[0:rows, 6 + i:7 + i]))
                    dve.tensor_scalar(prob[0:rows, i, 0:keys], prob[0:rows, i, 0:keys], tiny[0:rows, 9 + i:10 + i],
                                      None, ALU.mult).then_inc(pa_n, 1)
                if n:
                    dve.wait_ge(pa_hi, n)
                    dve.tensor_tensor(a_lo[:, n - 1, 0:TP], G[:, 2 + (n - 1) % 2, 0:TP],
                                      a_hi[:, n - 1, 0:TP].bitcast(f32), ALU.subtract).then_inc(pa_lo, 1)
            dve.wait_ge(pa_hi, NH)
            dve.tensor_tensor(a_lo[:, NH - 1, 0:TP], G[:, 2 + (NH - 1) % 2, 0:TP],
                              a_hi[:, NH - 1, 0:TP].bitcast(f32), ALU.subtract).then_inc(pa_lo, 1)

            dve.wait_ge(new_kept, 1)
            dve.wait_ge(qk_kept, DB)
            dve.wait_ge(mask_kept, 3)
            for b in range(DB):
                rows = s_buf[:, b].rearrange("p (g m q) -> p g m q", m=NH, q=DQ)
                far = mask_s[:, :, DQ * b:DQ * b + DQ].unsqueeze(2).to_broadcast([128, NPG + 1, NH, DQ])
                then(dve.tensor_tensor(rows, rows, far, ALU.add))
                dve.tensor_reduce(smax[:, 32 * b:32 * b + 32], s_buf[:, b].rearrange("p (g c) -> p c g", c=32),
                                  AX.X, ALU.max).then_inc(max_col, 1)
            dve.wait_ge(max_t, 1)
            dve.wait_ge(pa_o, NH)
            for a in range(2):
                then(dve.tensor_reduce(tiny[:, 12 + a:13 + a], A[:, 2, 128 * a:128 * a + 128], AX.X, ALU.max))
                dve.tensor_scalar(prob_t[:, a, 0:128], ident[:], tiny[:, 12 + a:13 + a], None,
                                  ALU.mult).then_inc(max_diag, 1)
            dve.wait_ge(max_all, 1)
            for b in range(DB):
                rows = s_buf[:, b].rearrange("p (g c) -> p g c", c=32)
                top = A[:, 3, 32 * b:32 * b + 32].unsqueeze(1).to_broadcast([128, NPG + 1, 32])
                dve.tensor_tensor(rows, rows, top, ALU.subtract).then_inc(s_shift, 1)
            for b in range(DB):
                dve.wait_ge(s_exp, b + 1)
                dve.tensor_reduce(smax[:, 32 * b:32 * b + 32], s_buf[:, b].rearrange("p (g c) -> p c g", c=32),
                                  AX.X, ALU.add).then_inc(s_colsum, 1)
            for n in range(OUT0, OUT0 + 3):
                lo(n)
            dve.wait_ge(s_den, 1)
            then(dve.reciprocal(win[:, 0, 0:256], A[:, 3, 256:512]))
            dve.wait_ge(v_used, NPAGES)
            dve.tensor_tensor(win[:, 1, 0:256], A[:, 0, 0:256], win[:, 0, 0:256], ALU.mult).then_inc(sa_n, 1)
            dve.wait_ge(sa_hi, 1)
            dve.wait_ge(sa_n, 1)
            dve.tensor_tensor(a_lo[:, :, TP:T].rearrange("p m (b q) -> p m b q", q=DQ),
                              win[:, 1, 0:256].rearrange("p (b m q) -> p m b q", m=NH, q=DQ),
                              a_hi[:, :, TP:T].rearrange("p m (b q) -> p m b q", q=DQ).bitcast(f32),
                              ALU.subtract).then_inc(sa_lo, 1)

            for n in range(OUT0 + 3, OUT0 + 8):
                lo(n)
            dve.wait_ge(x_again, 16)
            for s in range(NOUT):
                for n in range(OUT0 + 8 * s + 8, OUT0 + 8 * s + 10):
                    lo(n)
                for j in range(4):
                    wait_tile(dve, SLAB_OUT + s, j)
                    k = 4 * s + j
                    dve.scalar_tensor_tensor(out=z1[:, k], in0=z1[:, k], scalar=ALPHA, in1=G[:, j, 0:T],
                                             op0=ALU.mult, op1=ALU.add).then_inc(g_free, 1)
                for n in range(OUT0 + 8 * s + 10, OUT0 + 8 * s + (16 if s < 3 else 11)):
                    lo(n)

            def norm(z, tmp, round_, split):
                dve.wait_ge(mean_mm, round_ + 1)
                then(dve.tensor_scalar(tmp[:, 0], A[:, 1, 0:T], 1.0 / D, None, ALU.mult))
                for k in range(KB):
                    dve.tensor_tensor(z[:, k], z[:, k], tmp[:, 0], ALU.subtract).then_inc(centred, 1)
                dve.wait_ge(centred, KB * (round_ + 1))
                dve.wait_ge(sd_done, round_ + 1)
                then(dve.reciprocal(tmp[:, 0], tmp[:, 1]))
                for k in range(KB + 1):
                    if k < KB:
                        dve.tensor_tensor(z[:, k], z[:, k], tmp[:, 0], ALU.mult).then_inc(scaled, 1)
                    if split and k:
                        dve.wait_ge(x1_hi, k)
                        dve.tensor_tensor(x_lo[:, k - 1], z[:, k - 1], x_hi[:, k - 1].bitcast(f32),
                                          ALU.subtract).then_inc(x1_lo, 1)

            norm(z1, ln_a, 0, True)

            def lo_loop(i, n):
                c = position(n) % RING
                dve.wait_ge(hi_done, i * 8 + (n + 1))
                dve.tensor_tensor(w_lo[:, c], raw[:, c], w_hi[:, c].bitcast(f32), ALU.subtract).then_inc(lo_dve, 1)

            for n in range(UP0 + RING, UP0 + 6):
                lo(n)
            before = own[0]
            with dve.Fori(0, NUP) as i:
                def tap(j, w, step):
                    t = bass.ds(2 * i + (j % 2 + FB * (j // 2)), 1)
                    return dve.scalar_tensor_tensor(out=conv[:, j, 0:UO], in0=u_ext[:, j, w:w + UO],
                                                    scalar=cp_sb[:, t, w:w + 1].rearrange("p a w -> p (a w)"),
                                                    in1=conv[:, j, 0:UO], op0=ALU.mult, op1=ALU.add)

                for n in range(UP0 + 6, UP0 + 10):
                    lo_loop(i, n)
                for n in range(UP0 + 10, UP0 + 14):
                    for j in {UP0 + 10: (0, 1), UP0 + 11: (2, 3)}.get(n, ()):
                        dve.wait_ge(conv_a, i * 4 + (j + 1))
                        tap(j, 1, 0).then_inc(dve_own, 1)
                        dve.wait_ge(dve_own, i * 4 + (before + j + 1))
                        tap(j, 2, 0).then_inc(conv_v, 1)
                    if n == UP0 + 12:
                        dve.wait_ge(silu_done, i + 1)
                        dve.wait_ge(conv_v, i * 4 + 4)
                        dve.wait_ge(h_high, i * 2)
                        dve.tensor_tensor(gated[:, :, 0:UO], conv[:, 0:2, 0:UO], conv[:, 2:4, 0:UO],
                                          ALU.mult).then_inc(gated_done, 1)
                    if n == UP0 + 13:
                        dve.wait_ge(h_high, i * 2 + 2)
                        dve.wait_ge(gated_done, i + 1)
                        hh = h_hi[:, bass.ds(2 * i, 2), :].bitcast(f32)
                        hl = h_lo[:, bass.ds(2 * i, 2), :]
                        dve.tensor_tensor(hl[:, :, 0:TP], gated[:, :, 0:TP], hh[:, :, 0:TP],
                                          ALU.subtract).then_inc(h_split, 1)
                        dve.tensor_tensor(hl[:, :, TP:T].rearrange("p j (b q) -> p j b q", q=DQ),
                                          gated[:, :, US0:US0 + 6 * DB].rearrange("p j (b q) -> p j b q", q=6)[:, :, :, 0:DQ],
                                          hh[:, :, TP:T].rearrange("p j (b q) -> p j b q", q=DQ),
                                          ALU.subtract).then_inc(h_split, 1)
                    lo_loop(i, n)
            own[0] += 4 * NUP

            done = DN0 + 6
            for s in range(NDN):
                end = DN0 + DNC * (s + 1)
                for n in range(done, min(end + 2, END)):
                    lo(n)
                done = end + 2
                for j in range(4):
                    k = 4 * s + j
                    if j < 3:
                        dve.wait_ge(tile_done, 3 * (SLAB_DN + s) + j + 1)
                    else:
                        wait_used(dve, end - 1)
                    dve.wait_ge(residual, k + 1)
                    dve.scalar_tensor_tensor(out=z2[:, k], in0=z2[:, k], scalar=ALPHA, in1=G[:, j, 0:T],
                                             op0=ALU.mult, op1=ALU.add).then_inc(g_free, 1)
            dve.wait_ge(g_free, 4 * (SLAB_DN + NDN))
            norm(z2, ln_b, 1, False)


def constants():
    f = np.float32
    ident = np.eye(128, dtype=f)
    row = np.arange(128)
    e8 = (row[None, :] % IH == np.arange(IH)[:, None]).astype(f)
    w_scale = float(f(IH ** -0.5)) * ID ** -0.5
    sel = np.zeros((128, 2, TS), f)
    for g in range(2):
        sel[row, g, 16 * g + row // IH] = w_scale
    tok = np.arange(TS)
    keep = (tok[:, None] // DQ == tok[None, :] // DQ) & (tok[None, :] <= tok[:, None])
    new = np.stack([keep.astype(f), np.where(keep, 0, NEG).astype(f)], 1)
    pos = np.concatenate([np.arange(TP), PAST + np.tile(np.arange(DQ), DB)]).astype(f)
    rope = np.zeros((128, 4, T), f)
    for o, dim, half in ((0, ID, ID // 8), (2, HD, HD // 8)):
        freq = (THETA ** (-np.arange(half) / half)).astype(f)
        ang = (pos[None, :] * freq[:, None]).astype(np.float64)
        rope[:, o] = 1
        for base in range(0, 128, dim):
            rope[base:base + half, o] = rope[base + half:base + 2 * half, o] = np.cos(ang)
            rope[base:base + half, o + 1] = -np.sin(ang)
            rope[base + half:base + 2 * half, o + 1] = np.sin(ang)
    n = np.arange(16)
    count = np.stack([1 / np.minimum(w, n + 1) for w in WINS]).astype(f)
    return ident, e8, sel, new, rope, np.ascontiguousarray(np.broadcast_to(count, (128, 4, 16)))


def kernel(x_prompt, x_sample, cache_k, cache_v, cache_idx_k, state_pool, state_conv, page_table,
           meta_tokens, w_in, w_pool, pool_scale, w_out, ln1_g, ln1_b, w_up, conv_w, conv_b,
           w_down, ln2_g, ln2_b):
    import concourse.bacc as bacc
    from concourse.bass_utils import run_bass_kernel_spmd

    a = {k: np.asarray(v) for k, v in locals().items() if k not in ("bacc", "run_bass_kernel_spmd")}

    def chunks(w):
        k, n = w.shape
        return np.ascontiguousarray(w.reshape(k // 128, 128, n // CW, CW).transpose(2, 1, 0, 3)
                                    ).reshape(n // CW, 128, k // 128 // CK, CK * CW)

    def by_channel(v, *tail):
        return np.ascontiguousarray(np.moveaxis(v.reshape(*v.shape[:-1], -1, 128), (-1, -2), (0, 1)))

    x = np.concatenate([a["meta_tokens"], a["x_prompt"][0], a["x_sample"].reshape(TS, D)])
    wi = a["w_in"][0]
    q, k, v, iq, ik, p = (slice(0, 1024), slice(1024, 1536), slice(1536, 2048), slice(2048, 2560),
                          slice(2560, 2560 + IKW), slice(2560 + IKW, None))
    order = np.concatenate([np.arange(DFF).reshape(NUP, 256), DFF + np.arange(DFF).reshape(NUP, 256)], 1).reshape(-1)
    pool_ctx = np.zeros((128, 8, P_EXT), np.float32)
    pool_ctx[:, :, PS0:].reshape(128, 8, DB, CTX + DQ)[:, :, :, :CTX] = by_channel(a["state_pool"][0])
    conv_ctx = np.zeros((128, 2 * FB, 18), np.float32)
    conv_ctx[:, :, :16] = by_channel(a["state_conv"][0].reshape(16, 2 * DFF))
    ident, e8, sel, new, rope, count = constants()
    ins = dict(
        xT=by_channel(x).reshape(128, KB * T), w_iq=chunks(wi[:, iq])[0],
        w_ik=np.ascontiguousarray(wi[:, ik].reshape(KB, 128, IKW).transpose(1, 0, 2)).reshape(128, 2, 8 * IKW),
        w_in=chunks(np.concatenate([wi[:, q], wi[:, k], wi[:, v], wi[:, p]], 1)),
        w_out=chunks(a["w_out"][0]), w_up=chunks(a["w_up"][0][:, order]), w_down=chunks(a["w_down"][0]),
        kT_cache=np.ascontiguousarray(a["cache_k"][0].transpose(0, 3, 2, 1)).reshape(NPHYS, 128, 512),
        v_cache=np.ascontiguousarray(a["cache_v"][0]).reshape(NPHYS, 128, 512),
        ik_cache=np.ascontiguousarray(a["cache_idx_k"][0].transpose(0, 2, 1)),
        pages=np.ascontiguousarray(a["page_table"].reshape(1, NPAGES)),
        pool_ctx=pool_ctx, conv_ctx=conv_ctx,
        w_pool=np.ascontiguousarray(a["w_pool"][0].reshape(4, 2, 128, 256).transpose(2, 0, 1, 3)),
        pool_scale=by_channel(a["pool_scale"][0]),
        ln1=np.ascontiguousarray(np.stack([by_channel(a["ln1_g"][0]), by_channel(a["ln1_b"][0])], 1)),
        ln2=np.ascontiguousarray(np.stack([by_channel(a["ln2_g"][0]), by_channel(a["ln2_b"][0])], 1)),
        conv_p=by_channel(np.concatenate([a["conv_w"][0], a["conv_b"]])),
        ident_c=ident, e8_c=e8, sel_c=sel, new_c=new, rope_c=rope, count_c=count)
    outs = dict(yT=(128, KB, T), kT_out=(128, KVH, T), vT_out=(128, KVH, T), ikT_out=(ID, T),
                pT_out=(128, 8, P_EXT - P_OUT), cT_out=(128, 2 * FB, 18))
    nc = bacc.Bacc("TRN2", target_bir_lowering=False, num_devices=1)
    args = [nc.dram_tensor(f"in_{n}", v.shape, mybir.dt.from_np(v.dtype), kind="ExternalInput").ap()
            for n, v in ins.items()]
    args += [nc.dram_tensor(f"out_{n}", s, mybir.dt.float32, kind="ExternalOutput").ap() for n, s in outs.items()]
    layer(nc, *args)
    r = run_bass_kernel_spmd(nc, [{f"in_{n}": v for n, v in ins.items()}], core_ids=[0]).results[0]
    o = {n: np.asarray(r[f"out_{n}"]) for n in outs}

    def rows(t):
        return t.transpose(2, 1, 0).reshape(t.shape[2], -1)

    yy, kk, vv, pp, cc = rows(o["yT"]), rows(o["kT_out"]), rows(o["vT_out"]), rows(o["pT_out"]), rows(o["cT_out"])
    ii = o["ikT_out"].T
    heads = (KVH, HD)
    pool_s = pp[CTX:].reshape(DB, CTX + DQ, PW)[:, DQ:].copy()
    return (yy[META:TP][None].copy(), yy[TP:].reshape(DB, DQ, D).copy(),
            kk[:TP].reshape(1, 1, TP, *heads).copy(), vv[:TP].reshape(1, 1, TP, *heads).copy(),
            ii[:TP].reshape(1, 1, TP, ID).copy(), pp[:CTX][None, None].copy(), cc[0:2][None, None].copy(),
            kk[TP:].reshape(1, DB, DQ, *heads).copy(), vv[TP:].reshape(1, DB, DQ, *heads).copy(),
            ii[TP:].reshape(1, DB, DQ, ID).copy(), pool_s[None], cc[2:].reshape(1, DB, 2, 2 * DFF).copy())
```
